# Optimizing a Trainium2 kernel written in Bass

```python
import jax, jax.numpy as jnp
from jax import lax
import numpy as np

D_MODEL = 1024
BATCH = 1
SEQ = 2048
DEPTH = 2
DEC_BATCH = 1
DEC_SEQ = 64
PAST_LEN = 1024

CHUNK = 64
N_MIXERS = 2
E_A = D_MODEL
CONV_W = 31
CONV_STATE = CONV_W - 1
E_B = 2 * D_MODEL
H_B = 8
DH_B = E_B // H_B
SGU_CHUNK = 128
EPS = 1e-6
N_A = (DEPTH + 1) // 2
N_B = DEPTH // 2

kernel_name = "chunk_causal_conformer_gmlp_hybrid_step"

def rmsnorm(x, g):
    xf = x.astype(jnp.float32)
    y = xf * lax.rsqrt(jnp.mean(xf * xf, axis=-1, keepdims=True) + EPS)
    return (y * g.astype(jnp.float32)).astype(x.dtype)

def layernorm(x, g, b):
    xf = x.astype(jnp.float32)
    mu = jnp.mean(xf, axis=-1, keepdims=True)
    xc = xf - mu
    var = jnp.mean(xc * xc, axis=-1, keepdims=True)
    return (xc * lax.rsqrt(var + EPS) * g.astype(jnp.float32) + b.astype(jnp.float32)).astype(x.dtype)

def causal_dwconv(x_pad, w, b):
    out = lax.conv_general_dilated(
        x_pad, w[:, None, :].astype(x_pad.dtype), window_strides=(1,), padding='VALID',
        dimension_numbers=('NWC', 'WIO', 'NWC'), feature_group_count=x_pad.shape[-1])
    return out + b.astype(out.dtype)

def conv_mixer(h, hist, w_in, conv_w, conv_b, ln_g, ln_b, w_out):
    p = h @ w_in
    a, g_glu, z = jnp.split(p, 3, axis=-1)
    c = a * jax.nn.sigmoid(g_glu)
    c_pad = jnp.concatenate([hist.astype(c.dtype), c], axis=1)
    y = causal_dwconv(c_pad, conv_w, conv_b)
    y = jax.nn.silu(layernorm(y, ln_g, ln_b)) * jax.nn.silu(z)
    return y @ w_out, c_pad[:, -CONV_STATE:]

def block_causal_mask(n):
    cid = jnp.arange(n) // CHUNK
    return cid[None, :] <= cid[:, None]

def sgu_mixer(h, chunk_len, w_in, ln_g, ln_b, w_s, s_bias, w_out):
    B, T, _ = h.shape
    p = h @ w_in
    uv = jax.nn.gelu(p[..., :2 * E_B], approximate=False)
    z = p[..., 2 * E_B:]
    u, v = jnp.split(uv, 2, axis=-1)
    v = layernorm(v, ln_g, ln_b)
    nc = T // chunk_len
    u5 = u.reshape(B, nc, chunk_len, H_B, DH_B)
    v5 = v.reshape(B, nc, chunk_len, H_B, DH_B)
    ws = jnp.where(block_causal_mask(chunk_len)[None], w_s[:, :chunk_len, :chunk_len], 0).astype(v.dtype)
    mixed = jnp.einsum('gij,bcjgd->bcigd', ws, v5)
    mixed = mixed + jnp.transpose(s_bias[:, :chunk_len]).astype(v.dtype)[None, None, :, :, None]
    s = (u5 * mixed).reshape(B, T, E_B) * jax.nn.silu(z)
    return s @ w_out, v

def setup_inputs(seed: int = 0) -> dict:
    key = jax.random.key(seed)
    ks = jax.random.split(key, 20)
    f32 = jnp.float32
    n = jax.random.normal
    return {
        "x_prompt": n(ks[0], (BATCH, SEQ, D_MODEL), f32),
        "x_sample": n(ks[1], (DEC_BATCH, DEC_SEQ, D_MODEL), f32),
        "state_conv": n(ks[2], (N_A, DEC_BATCH, CONV_STATE, E_A), f32) * 0.5,
        "pre_norm_g": 1.0 + 0.02 * n(ks[3], (DEPTH, D_MODEL), f32),
        "post_norm_g": 1.0 + 0.02 * n(ks[4], (DEPTH, D_MODEL), f32),
        "a_w_in": n(ks[5], (N_A, D_MODEL, 3 * E_A), f32) * D_MODEL ** -0.5,
        "a_conv_w": n(ks[6], (N_A, CONV_W, E_A), f32) * CONV_W ** -0.5,
        "a_conv_b": 0.02 * n(ks[7], (N_A, E_A), f32),
        "a_ln_g": 1.0 + 0.02 * n(ks[8], (N_A, E_A), f32),
        "a_ln_b": 0.02 * n(ks[9], (N_A, E_A), f32),
        "a_w_out": n(ks[10], (N_A, E_A, D_MODEL), f32) * E_A ** -0.5,
        "b_w_in": n(ks[11], (N_B, D_MODEL, 3 * E_B), f32) * D_MODEL ** -0.5,
        "b_ln_g": 1.0 + 0.02 * n(ks[12], (N_B, E_B), f32),
        "b_ln_b": 0.02 * n(ks[13], (N_B, E_B), f32),
        "b_w_s": n(ks[14], (N_B, H_B, SGU_CHUNK, SGU_CHUNK), f32) * SGU_CHUNK ** -0.5,
        "b_s_bias": 1.0 + 0.02 * n(ks[15], (N_B, H_B, SGU_CHUNK), f32),
        "b_w_out": n(ks[16], (N_B, E_B, D_MODEL), f32) * E_B ** -0.5,
    }

def reference(x_prompt, x_sample, state_conv, pre_norm_g, post_norm_g,
              a_w_in, a_conv_w, a_conv_b, a_ln_g, a_ln_b, a_w_out,
              b_w_in, b_ln_g, b_ln_b, b_w_s, b_s_bias, b_w_out):
    xp, xs = x_prompt, x_sample
    conv_p, conv_s, v_s = [], [], []
    dec_len = xs.shape[1]
    for i in range(DEPTH):
        j = i // N_MIXERS
        hp = rmsnorm(xp, pre_norm_g[i])
        hs = rmsnorm(xs, pre_norm_g[i])
        if i % N_MIXERS == 0:
            zero_hist = jnp.zeros((xp.shape[0], CONV_STATE, E_A), xp.dtype)
            op, cp = conv_mixer(hp, zero_hist, a_w_in[j], a_conv_w[j], a_conv_b[j],
                                a_ln_g[j], a_ln_b[j], a_w_out[j])
            os_, cs = conv_mixer(hs, state_conv[j], a_w_in[j], a_conv_w[j], a_conv_b[j],
                                 a_ln_g[j], a_ln_b[j], a_w_out[j])
            conv_p.append(cp)
            conv_s.append(cs)
        else:
            op, _ = sgu_mixer(hp, SGU_CHUNK, b_w_in[j], b_ln_g[j], b_ln_b[j],
                              b_w_s[j], b_s_bias[j], b_w_out[j])
            os_, vs = sgu_mixer(hs, dec_len, b_w_in[j], b_ln_g[j], b_ln_b[j],
                                b_w_s[j], b_s_bias[j], b_w_out[j])
            v_s.append(vs)
        xp = xp + rmsnorm(op, post_norm_g[i])
        xs = xs + rmsnorm(os_, post_norm_g[i])
    new_conv_prompt = jnp.stack(conv_p)
    new_conv_sample = jnp.stack(conv_s)
    new_sgu_v_sample = jnp.stack(v_s)
    return (xp, xs, new_conv_prompt, new_conv_sample, new_sgu_v_sample)


_drawn_inputs = setup_inputs


def setup_inputs(seed=0):
    import zlib

    import numpy as np

    out = dict(_drawn_inputs(seed))
    spreads = {}
    factors = {'post_norm_g': 2.692,
     'a_ln_g': 2.868,
     'a_ln_b': 3.126,
     'b_ln_g': 2.904,
     'b_ln_b': 2.776,
     'b_s_bias': 6.014}
    for name, (base, spread) in spreads.items():
        noise = np.random.default_rng([zlib.crc32(name.encode()), seed]).standard_normal(out[name].shape)
        drawn = base * np.exp(spread * noise) if base else spread * noise
        out[name] = __import__('jax').numpy.asarray(drawn.astype(out[name].dtype))
    for name, factor in factors.items():
        out[name] = (out[name] * factor).astype(out[name].dtype)
    return out
```

```python
from contextlib import ExitStack

import concourse.bass as bass
from concourse import mybir

P = 128
D = 1024
EA = 1024
EB = 2048
N_PROMPT, N_SAMPLE = 2048, 64
NT = N_PROMPT + N_SAMPLE
TAPS = 31
HIST = TAPS - 1
GROUPS = 8
KD = D // P
KB = EB // P
TILES = NT // P
LAST = TILES
CHUNKS = [(0, 424), (424, 424), (848, 424), (1272, 424), (1696, 416)]
NC = len(CHUNKS)
CW = max(w for _, w in CHUNKS)
PADDED = HIST + N_PROMPT + HIST + N_SAMPLE
CONVW = PADDED - HIST
JA = EA // P
VQ = 256
NQ = EB // VQ
EPS = 1e-6
P_CONVB, P_LNG, P_LNB, P_BG, P_BB = 0, 8, 16, 24, 40
NPAR = 56


class Step:

    def __init__(self, k, c):
        self.k, self.c = k, c

    @property
    def v(self):
        return self.c if self.k is None else 2 * self.k + self.c

    @property
    def half(self):
        return self.c // 2 if self.k is None else self.k + self.c // 2

    @property
    def par(self):
        return self.c % 2

    @property
    def rows(self):
        return N_SAMPLE if self.k is None and self.c == LAST else P

    def __add__(self, n):
        return Step(self.k, self.c + n)

    def among(self, lo, hi):
        return self.k is not None or lo <= self.c < hi


def pipeline(engine, step, first, last, loop_first, pairs):
    for i in range(first, loop_first):
        step(Step(None, i))
    if pairs:
        with engine.Fori(0, pairs) as k:
            step(Step(k, loop_first))
            step(Step(k, loop_first + 1))
    for i in range(loop_first + 2 * pairs, last):
        step(Step(None, i))


def build(nc, x, wa_in, wa_out, wb_v, wb_uz, wb_out, conv_par, chan_par, pre_g, post_g, b_gb, ws_t, s_bias,
          consts, y_out, conv_out, v_out):
    fp32 = mybir.dt.float32
    f32r = mybir.dt.float32r
    ALU = mybir.AluOpType
    ACT = mybir.ActivationFunctionType

    y_d = nc.dram_tensor("y_scratch", [EA, NT], fp32).ap()
    zs_d = nc.dram_tensor("silu_z_scratch", [EA, NT], fp32).ap()
    x1_d = nc.dram_tensor("x1_scratch", [NT, D], fp32).ap()
    v_d = nc.dram_tensor("v_scratch", [NT, EB], fp32).ap()
    s_d = nc.dram_tensor("s_scratch", [EB, NT], fp32).ap()
    y_v = y_d.rearrange("(k p) n -> p k n", p=P)
    zs_v = zs_d.rearrange("(k p) n -> p k n", p=P)
    s_v = s_d.rearrange("(k p) n -> p k n", p=P)
    v_v = v_d[0:N_PROMPT, :].rearrange("(t p) c -> p t c", p=P)

    ctx = ExitStack()
    with ctx:
        base = (nc.sbuf_base + 31) // 32 * 32
        top = nc.sbuf_usable_end // 32 * 32

        class Region:

            def __init__(self, at, end):
                self.at, self.end = at, end

            def __call__(self, name, shape, dt=fp32):
                n = 4
                for s in shape[1:]:
                    n *= s
                t = nc.alloc_sbuf_tensor_at(name, shape, dt, offset=self.at)
                self.at += (n + 31) // 32 * 32
                assert self.at <= self.end, (name, self.at, self.end)
                return t

        def sem(name):
            return ctx.enter_context(nc.semaphore(name))

        g = Region(base, top)
        con = g("con", [P, 2 * P])
        ident, ones = con[:, 0:P], con[:, P:2 * P]
        par = g("par", [P, NPAR])
        ss = g("ss", [P, 2])
        rn = g("rn", [P, 2])
        half_neg = g("half_neg", [P, TILES + 1])
        h_at = g.at
        h_bytes = 2 * KD * NT * 4
        free_at = h_at + h_bytes

        r = Region(h_at, free_at)
        Hh = r("Hh", [P, KD, NT], f32r)
        Hl = r("Hl", [P, KD, NT], f32r)

        r = Region(free_at, top)
        xt = [r(f"xt{i}", [P, D]) for i in range(2)]
        xn = [r(f"xn{i}", [P, D]) for i in range(2)]
        sq = r("sq", [P, D])
        gpre = r("gpre", [P, D])
        norm_end = r.at

        r = Region(free_at, top)
        cp = [r(f"cp{i}", [P, PADDED]) for i in range(2)]
        acc = [r(f"acc{i}", [P, CONVW]) for i in range(2)]
        zc = [r(f"zc{i}", [P, CW]) for i in range(2)]
        raw = [r(f"raw{i}", [P, KD * P]) for i in range(2)]
        Wh = [r(f"Wh{i}", [P, KD, P], f32r) for i in range(3)]
        Wl = [r(f"Wl{i}", [P, KD, P], f32r) for i in range(3)]
        cpar = r("cpar", [P, JA, HIST + TAPS])
        cj = r("cj", [P, 2, HIST + TAPS])
        stout = r("stout", [P, JA, 2 * HIST])

        r = Region(h_at, free_at)
        Woh = r("Woh", [P, KD, D], f32r)
        Wol = r("Wol", [P, KD, D], f32r)
        yb = [r(f"yb{i}", [P, KD, P]) for i in range(2)]
        zb = [r(f"zb{i}", [P, KD, P]) for i in range(2)]
        sh = [r(f"sh{i}", [P, KD, P], f32r) for i in range(2)]
        sl = [r(f"sl{i}", [P, KD, P], f32r) for i in range(2)]
        xb = [r(f"xb{i}", [P, D]) for i in range(2)]
        x1 = [r(f"x1{i}", [P, D]) for i in range(2)]
        sq3 = r("sq3", [P, D])
        gpa = r("gpa", [P, D])
        dg = r("dg", [P, 2, P])
        bst = r("bst", [P, 2, 6])
        mv = r("mv", [P, 2, 2])
        rs3 = r("rs3", [P, 2])
        rm3 = r("rm3", [P, 2])
        ss3 = r("ss3", [P, 2])
        r23 = r("r23", [P, 2])

        r = Region(norm_end, top)
        rv = r("rv", [P, KD * VQ])
        Vh = [r(f"Vh{i}", [P, KD, VQ], f32r) for i in range(2)]
        Vl = [r("Vl0", [P, KD, VQ], f32r)]
        r5 = Region(free_at, norm_end)
        Vl.append(r5("Vl1", [P, KD, VQ], f32r))
        vb = [r5(f"vb{i}", [P, VQ]) for i in range(5)]
        vbs = r("vbs", [P, TILES + 1, NQ, 6])
        keep = Region(top - 1024, top)
        vmv = keep("vmv", [P, TILES + 1, 2])
        vrs = keep("vrs", [P, TILES + 1])
        assert r.at <= top - 1024

        r = Region(free_at, top - 1024)
        raw6 = [r(f"raw6{i}", [P, KD * P]) for i in range(2)]
        Uh = [r(f"Uh{i}", [P, KD, P], f32r) for i in range(2)]
        Ul = [r(f"Ul{i}", [P, KD, P], f32r) for i in range(2)]
        vt = r("vt", [P, TILES + 1, P])
        m6 = [r(f"m6{i}", [P, NT]) for i in range(2)]
        ugc = [r(f"ugc{i}", [P, CW]) for i in range(2)]
        zc6 = [r(f"zc6{i}", [P, CW]) for i in range(2)]
        wst = r("wst", [P, GROUPS, P])
        rsb = r("rsb", [P, GROUPS, P])
        sbb = r("sbb", [P, GROUPS, P])
        addj = r("addj", [P, P])
        gb = r("gb", [N_SAMPLE, 2, P])
        vo = r("vo", [N_SAMPLE, P])

        r = Region(h_at, free_at)
        Wbh = r("Wbh", [P, KB, D], f32r)
        Wbl = r("Wbl", [P, KB, D], f32r)
        r = Region(free_at, top)
        raw7 = [r(f"raw7{i}", [P, D]) for i in range(2)]
        st7 = [r(f"st7{i}", [P, KB, P]) for i in range(2)]
        s7h = [r(f"s7h{i}", [P, KB, P], f32r) for i in range(2)]
        s7l = [r(f"s7l{i}", [P, KB, P], f32r) for i in range(2)]
        x7 = [r(f"x7{i}", [P, D]) for i in range(2)]
        t7 = r("t7", [P, D])
        gpb = r("gpb", [P, D])
        r7 = Region(h_at + 2 * KB * D * 4, free_at)
        ss7 = r7("ss7", [P, 2])
        r27 = r7("r27", [P, 2])

        PS = ctx.enter_context(nc.psum_tensor("PS", [P, 8, 512], fp32))

        def banks(b, n=2):
            return PS[:, b:b + n, :].rearrange("p b n -> p (b n)")

        passed = {e: sem(f"passed_{e}") for e in ("Pool", "DVE", "PE")}

        def apart(engine, name):
            engine.sem_inc(passed[name], 1)

        ld_con = sem("ld_con")
        c_neg = sem("c_neg")
        norm_sems = [{n: sem(f"n{i}_{n}") for n in
                      ("ld0", "ld1", "g", "sq", "eps", "r", "scaled", "tr", "hi", "lo")} for i in range(2)]
        a_raw = [sem(f"a_raw{i}") for i in range(2)]
        ld_cpar = sem("ld_cpar")
        a_hi, a_lo, a_mm = sem("a_hi"), sem("a_lo"), sem("a_mm")
        a_sig, a_prod, a_zs = sem("a_sig"), sem("a_prod"), sem("a_zs")
        a_pad, a_cj, a_tap, a_conv, a_state = sem("a_pad"), sem("a_cj"), sem("a_tap"), sem("a_conv"), sem("a_state")
        a_zst = [sem(f"a_zst{i}") for i in range(2)]
        a_yst = [sem(f"a_yst{i}") for i in range(2)]
        out_conv = sem("out_conv")
        o_raw = [sem(f"o_raw{i}") for i in range(2)]
        o_hi, o_lo = sem("o_hi"), sem("o_lo")
        o_g = sem("o_g")
        o_ldy = [sem(f"o_ldy{i}") for i in range(2)]
        o_ldz = [sem(f"o_ldz{i}") for i in range(2)]
        o_ldx = [sem(f"o_ldx{i}") for i in range(2)]
        o_ytr, o_bn, o_agg, o_eps, o_rs, o_rm, o_dg, o_bc = (sem(f"o_{n}") for n in
            ("ytr", "bn", "agg", "eps", "rs", "rm", "dg", "bc"))
        o_nr, o_nrm, o_sil, o_sz, o_sh, o_sl, o_main = (sem(f"o_{n}") for n in
            ("nr", "nrm", "sil", "sz", "sh", "sl", "main"))
        o_sq, o_eps2, o_r2, o_pm, o_post = (sem(f"o_{n}") for n in ("sq", "eps2", "r2", "pm", "post"))
        o_st = [sem(f"o_st{i}") for i in range(2)]
        v_ld, v_hi, v_lo, v_mm, v_gel, v_bn = (sem(f"v_{n}") for n in ("ld", "hi", "lo", "mm", "gel", "bn"))
        v_st = [sem(f"v_st{i}") for i in range(5)]
        v_zero, v_agg, v_eps, v_rs = (sem(f"v_{n}") for n in ("zero", "agg", "eps", "rs"))
        u_raw = [sem(f"u_raw{i}") for i in range(2)]
        u_hi, u_lo, u_mm, u_gel, u_silu, u_mu, u_mz = (sem(f"u_{n}") for n in
            ("hi", "lo", "mm", "gel", "silu", "mu", "mz"))
        u_ws, u_mask, u_rsmm, u_rsb, u_sbb = (sem(f"u_{n}") for n in ("ws", "mask", "rsmm", "rsb", "sbb"))
        u_ldv, u_gb, u_sub, u_vn, u_vom, u_vo, u_add, u_mix, u_mev = (sem(f"u_{n}") for n in
            ("ldv", "gb", "sub", "vn", "vom", "vo", "add", "mix", "mev"))
        u_sst = [sem(f"u_sst{i}") for i in range(2)]
        u_vst = sem("u_vst")
        b_raw = [sem(f"b_raw{i}") for i in range(2)]
        b_hi, b_lo, b_g = sem("b_hi"), sem("b_lo"), sem("b_g")
        b_lds = [sem(f"b_lds{i}") for i in range(2)]
        b_ldx = [sem(f"b_ldx{i}") for i in range(2)]
        b_sh, b_sl, b_main, b_sq, b_eps, b_r2, b_pm, b_post = (sem(f"b_{n}") for n in
            ("sh", "sl", "main", "sq", "eps", "r2", "pm", "post"))
        b_st = [sem(f"b_st{i}") for i in range(2)]

        block = ctx.enter_context(nc.Block())

        def rows_of(dram, t):
            if t.k is None:
                return dram[t.c * P:t.c * P + t.rows, :]
            return dram[bass.ds(t.v * P, P), :]

        def cols_of(view, t):
            if t.k is None:
                return view[:, :, t.c * P:t.c * P + t.rows]
            return view[:, :, bass.ds(t.v * P, P)]

        def norm_loads(sp, s, src, gain, first_wait):
            def step(t):
                if t.among(2, LAST + 1):
                    sp.wait_ge(s["scaled"], t.v - 1)
                sp.dma_start(xt[t.par][0:t.rows, :], rows_of(src, t)).then_inc(s[f"ld{t.par}"], 16)
            first_wait()
            sp.dma_start(gpre[:, :], gain.to_broadcast([P, D])).then_inc(s["g"], 16)
            pipeline(nc.sync, step, 0, LAST + 1, 2, 7)

        @block.sync
        def _(sp):
            sp.dma_start(con[:, :], consts).then_inc(ld_con, 16)
            sp.dma_start(par[:, :], chan_par).then_inc(ld_con, 16)
            norm_loads(sp, norm_sems[0], x, pre_g[0:1, :], lambda: None)

            sp.wait_ge(norm_sems[0]["lo"], LAST + 1)
            sp.dma_start(cpar[:, :, :], conv_par).then_inc(ld_cpar, 16)

            def a_load(j, m):
                n = 3 * j.v + m
                last = {0: n, 1: n - 2, 2: n - 1}[m]
                if j.among(1, JA) or m == 2:
                    sp.wait_ge(a_hi, last)
                    sp.wait_ge(a_lo, last)
                sp.dma_start(raw[m % 2][:, :], wa_in[n, :, :]).then_inc(a_raw[m % 2], 16)

            pipeline(nc.sync, lambda j: [a_load(j, m) for m in range(3)], 0, JA, 1, 3)

            for k in range(KD):
                last = 3 * JA if k < 2 else None
                if last:
                    sp.wait_ge(a_hi, last)
                    sp.wait_ge(a_lo, last)
                else:
                    sp.wait_ge(o_hi, k - 1)
                    sp.wait_ge(o_lo, k - 1)
                sp.dma_start(raw[k % 2][:, :], wa_out[k * P:(k + 1) * P, :]).then_inc(o_raw[k % 2], 16)
            sp.wait_ge(a_mm, 3 * NC * JA)
            sp.dma_start(gpa[:, :], post_g[0:1, :].to_broadcast([P, D])).then_inc(o_g, 16)
            for i in range(2):
                sp.wait_ge(a_yst[i], 32 * JA // 2)
                sp.wait_ge(a_zst[i], 16 * NC * JA // 2)

            def o_load(i):
                if i.among(0, LAST + 1):
                    t = i
                    if t.among(2, LAST + 1):
                        sp.wait_ge(o_sz, t.v - 1)
                    sp.dma_start(yb[t.par][:, :, 0:t.rows], cols_of(y_v, t)).then_inc(o_ldy[t.par], 16)
                    if t.among(2, LAST + 1):
                        sp.wait_ge(o_sl, t.v - 1)
                    sp.dma_start(zb[t.par][:, :, 0:t.rows], cols_of(zs_v, t)).then_inc(o_ldz[t.par], 16)
                if i.among(1, LAST + 2):
                    t = i + (-1)
                    if t.among(2, LAST + 1):
                        sp.wait_ge(o_post, t.v - 1)
                    sp.dma_start(xb[t.par][0:t.rows, :], rows_of(x, t)).then_inc(o_ldx[t.par], 16)

            pipeline(nc.sync, o_load, 0, LAST + 2, 3, 6)

            def x1_stored():
                sp.wait_ge(o_st[0], 16 * (LAST // 2 + 1))
                sp.wait_ge(o_st[1], 16 * (LAST // 2))
            norm_loads(sp, norm_sems[1], x1_d, pre_g[1:2, :], x1_stored)

            def v_load(q):
                if q.among(1, NQ):
                    sp.wait_ge(v_hi, q.v)
                    sp.wait_ge(v_lo, q.v)
                sp.dma_start(rv[:, :], wb_v[q.v, :, :]).then_inc(v_ld, 16)

            def v_step(q):
                if q.among(0, NQ - 1):
                    v_load(q + 1)
                for t in range(LAST + 1):
                    rows = N_SAMPLE if t == LAST else P
                    slot = 4 if t == LAST else t % 4
                    sp.wait_ge(v_gel, (LAST + 1) * q.v + t + 1)
                    c0 = bass.ds(q.v * VQ, VQ)
                    sp.dma_start(v_d[t * P:t * P + rows, c0], vb[slot][0:rows, :]).then_inc(v_st[slot], 16)

            v_load(Step(None, 0))
            pipeline(nc.sync, v_step, 0, NQ, 1, 3)

            sp.wait_ge(v_agg, LAST + 2)
            for s in range(4):
                sp.wait_ge(v_st[s], 16 * 4 * NQ)
            sp.wait_ge(v_st[4], 16 * NQ)
            sp.dma_start(wst[:, :, :], ws_t).then_inc(u_ws, 16)
            sp.dma_start(sbb[:, :, :].rearrange("p a b -> p (a b)"),
                         s_bias.to_broadcast([P, GROUPS * P])).then_inc(u_sbb, 16)

            def u_load(j, m):
                n = 2 * j.v + m
                if j.among(1, KB):
                    sp.wait_ge(u_hi, n - 1)
                    sp.wait_ge(u_lo, n - 1)
                sp.dma_start(raw6[m][:, :], wb_uz[n, :, :]).then_inc(u_raw[m], 16)

            def u_step(j):
                u_load(j, 0)
                u_load(j, 1)
                if j.among(1, KB):
                    sp.wait_ge(u_mix, 5 * j.v)
                    sp.wait_ge(u_vo, j.v)
                c0 = bass.ds(j.v * P, P)
                sp.dma_start(vt[:, 0:TILES, :], v_v[:, :, c0]).then_inc(u_ldv, 16)
                sp.dma_start(vt[0:N_SAMPLE, LAST, :], v_d[N_PROMPT:NT, c0]).then_inc(u_ldv, 16)
                for i in range(2):
                    sp.dma_start(gb[:, i, :], b_gb[i:i + 1, c0].to_broadcast([N_SAMPLE, P])).then_inc(u_gb, 16)

            pipeline(nc.sync, u_step, 0, KB, 2, 7)

            sp.wait_ge(u_mm, 2 * NC * KB)
            sp.wait_ge(u_mz, NC * KB)
            for i in range(2):
                sp.wait_ge(u_sst[i], 16 * KB // 2)
            sp.wait_ge(u_vst, 16 * KB)
            for k in range(2):
                sp.dma_start(raw7[k][:, :], wb_out[k * P:(k + 1) * P, :]).then_inc(b_raw[k], 16)
            sp.dma_start(gpb[:, :], post_g[1:2, :].to_broadcast([P, D])).then_inc(b_g, 16)

            def b_load(t):
                if t.among(2, LAST + 1):
                    sp.wait_ge(b_sl, t.v - 1)
                sp.dma_start(st7[t.par][:, :, 0:t.rows], cols_of(s_v, t)).then_inc(b_lds[t.par], 16)
                if t.among(2, LAST + 1):
                    sp.wait_ge(b_st[t.par], 16 * t.half)
                sp.dma_start(x7[t.par][0:t.rows, :], rows_of(x1_d, t)).then_inc(b_ldx[t.par], 16)

            b_load(Step(None, 0))
            for k in range(2, KB):
                sp.wait_ge(b_hi, k - 1)
                sp.wait_ge(b_lo, k - 1)
                sp.dma_start(raw7[k % 2][:, :], wb_out[k * P:(k + 1) * P, :]).then_inc(b_raw[k % 2], 16)
            pipeline(nc.sync, b_load, 1, LAST + 1, 2, 7)

        def rsqrt(pool, src, dst, rows, added, done, count):
            apart(pool, "Pool")
            nc.gpsimd.tensor_scalar(src[0:rows], src[0:rows], EPS, None, ALU.add).then_inc(added, 1)
            pool.wait_ge(added, count)
            nc.gpsimd.tensor_tensor(dst[0:rows], src[0:rows], half_neg[0:rows, 0:1], ALU.pow).then_inc(done, 1)

        def norm_pool(pool, s):
            def step(t):
                pool.wait_ge(s["sq"], t.v + 1)
                rsqrt(pool, ss[:, t.par:t.par + 1], rn[:, t.par:t.par + 1], t.rows, s["eps"], s["r"], t.v + 1)
            pipeline(nc.gpsimd, step, 0, LAST + 1, 0, 8)

        @block.gpsimd
        def _(pool):
            nc.gpsimd.memset(half_neg[:, :], -0.5).then_inc(c_neg, 1)
            pool.wait_ge(c_neg, 1)
            norm_pool(pool, norm_sems[0])

            def a_store(j):
                if j.among(1, JA + 1):
                    jj = j + (-1)
                    pool.wait_ge(a_conv, j.v)
                    rows = bass.ds(jj.v * P, P)
                    apart(pool, "Pool")
                    nc.gpsimd.dma_start(y_d[rows, 0:N_PROMPT], acc[jj.par][:, 0:N_PROMPT]).then_inc(a_yst[jj.par], 16)
                    nc.gpsimd.dma_start(y_d[rows, N_PROMPT:NT],
                                        acc[jj.par][:, N_PROMPT + HIST:CONVW]).then_inc(a_yst[jj.par], 16)
                if j.among(0, JA):
                    for c, (c0, w) in enumerate(CHUNKS):
                        slot = (NC * j.c + c) % 2
                        pool.wait_ge(a_zs, NC * j.v + c + 1)
                        apart(pool, "Pool")
                        nc.gpsimd.dma_start(zs_d[bass.ds(j.v * P, P), c0:c0 + w], zc[slot][:, 0:w])\
                            .then_inc(a_zst[slot], 16)

            pipeline(nc.gpsimd, a_store, 0, JA + 1, 1, 3)
            pool.wait_ge(a_state, 2 * JA)
            nc.gpsimd.dma_start(conv_out, stout[:, :, :]).then_inc(out_conv, 16)

            def o_step(i):
                if i.among(1, LAST + 2):
                    t = i + (-1)
                    pool.wait_ge(o_sq, t.v + 1)
                    rsqrt(pool, ss3[:, t.par:t.par + 1], r23[:, t.par:t.par + 1], t.rows, o_eps2, o_r2, t.v + 1)
                if i.among(-2, LAST - 1):
                    t = i + 2
                    pool.wait_ge(o_agg, t.v + 1)
                    rsqrt(pool, mv[:, t.par, 1:2], rs3[:, t.par:t.par + 1], t.rows, o_eps, o_rs, t.v + 1)
                if i.among(1, LAST + 2):
                    t = i + (-1)
                    pool.wait_ge(o_post, t.v + 1)
                    apart(pool, "Pool")
                    nc.gpsimd.dma_start(rows_of(x1_d, t), x1[t.par][0:t.rows, :]).then_inc(o_st[t.par], 16)

            pipeline(nc.gpsimd, o_step, -2, LAST + 2, 3, 5)
            norm_pool(pool, norm_sems[1])

            pool.wait_ge(v_agg, LAST + 2)
            nc.gpsimd.tensor_scalar(vmv[:, :, 1], vmv[:, :, 1], EPS, None, ALU.add).then_inc(v_eps, 1)
            pool.wait_ge(v_eps, 1)
            nc.gpsimd.tensor_tensor(vrs[:, :], vmv[:, :, 1], half_neg[:, :], ALU.pow).then_inc(v_rs, 1)

            def u_store(j):
                if j.among(0, KB):
                    pool.wait_ge(u_vo, j.v + 1)
                    apart(pool, "Pool")
                    nc.gpsimd.dma_start(v_out[:, bass.ds(j.v * P, P)], vo[:, :]).then_inc(u_vst, 16)
                if j.among(1, KB + 1):
                    jj = j + (-1)
                    pool.wait_ge(u_mz, NC * j.v)
                    apart(pool, "Pool")
                    nc.gpsimd.dma_start(s_d[bass.ds(jj.v * P, P), :], m6[jj.par][:, :]).then_inc(u_sst[jj.par], 16)

            pipeline(nc.gpsimd, u_store, 0, KB + 1, 1, 7)

            def b_step(t):
                pool.wait_ge(b_sq, t.v + 1)
                rsqrt(pool, ss7[:, t.par:t.par + 1], r27[:, t.par:t.par + 1], t.rows, b_eps, b_r2, t.v + 1)
                pool.wait_ge(b_post, t.v + 1)
                apart(pool, "Pool")
                nc.gpsimd.dma_start(rows_of(y_out, t), x7[t.par][0:t.rows, :]).then_inc(b_st[t.par], 16)

            pipeline(nc.gpsimd, b_step, 0, LAST + 1, 0, 8)
            pool.wait_ge(out_conv, 16)
            pool.wait_ge(u_vst, 16 * KB)
            pool.wait_ge(b_st[0], 16 * (LAST // 2 + 1))
            pool.wait_ge(b_st[1], 16 * (LAST // 2))

        def square_mean(out, src, acc_out, done):
            nc.scalar.activation(out, src, ACT.Square, scale=D ** -0.5, accum_out=acc_out).then_inc(done, 1)

        def norm_act(act, s):
            def step(i):
                if i.among(-1, LAST):
                    t = i + 1
                    act.wait_ge(s[f"ld{t.par}"], 16 * t.half + 16)
                    if t.among(1, LAST + 1):
                        act.wait_ge(s["sq"], t.v)
                    square_mean(sq[0:t.rows, :], xt[t.par][0:t.rows, :], ss[0:t.rows, t.par:t.par + 1], s["sq"])
                if i.among(0, LAST + 1):
                    t = i
                    act.wait_ge(s["tr"], t.v + 1)
                    src = banks(2 * t.par).rearrange("p (k n) -> p k n", k=KD)[:, :, 0:t.rows]
                    nc.scalar.activation(tile_of(Hh, t), src, ACT.Copy).then_inc(s["hi"], 1)
            pipeline(nc.scalar, step, -1, LAST + 1, 0, 7)

        def tile_of(h, t):
            if t.k is None:
                return h[:, :, t.c * P:t.c * P + t.rows]
            return h[:, :, bass.ds(t.v * P, P)]

        def padded(c0, w):
            if c0 + w <= N_PROMPT:
                return [(0, HIST + c0, w)]
            w0 = N_PROMPT - c0
            return [(0, HIST + c0, w0), (w0, HIST + N_PROMPT + HIST, w - w0)]

        def b_hi_split(act, t):
            act.wait_ge(b_lds[t.par], 16 * t.half + 16)
            if t.among(2, LAST + 1):
                act.wait_ge(b_main, t.v - 1)
            nc.scalar.activation(s7h[t.par][:, :, 0:t.rows], st7[t.par][:, :, 0:t.rows], ACT.Copy).then_inc(b_sh, 1)

        @block.scalar
        def _(act):
            norm_act(act, norm_sems[0])

            def a_hi_split(j, m):
                n = 3 * j.v + m
                act.wait_ge(a_raw[m % 2], 16 * (j.v + 1) if m == 1 else 16 * (2 * j.v + m // 2 + 1))
                if j.among(1, JA):
                    act.wait_ge(a_mm, NC * (n - 2))
                nc.scalar.activation(Wh[m][:, :, :].rearrange("p k n -> p (k n)"), raw[m % 2][:, :], ACT.Copy)\
                    .then_inc(a_hi, 1)

            def a_step(j):
                a_hi_split(j, 2)
                if j.among(2, JA):
                    act.wait_ge(a_conv, j.v - 1)
                    act.wait_ge(a_state, 2 * j.v - 2)
                for c, (c0, w) in enumerate(CHUNKS):
                    act.wait_ge(a_mm, 3 * NC * j.v + c + 1)
                    for f, to, n in (ps := padded(c0, w)):
                        last = nc.scalar.activation(cp[j.par][:, to:to + n], PS[:, c, f:f + n], ACT.Sigmoid)
                    last.then_inc(a_sig, 1)
                if j.among(0, JA - 1):
                    a_hi_split(j + 1, 0)
                    a_hi_split(j + 1, 1)
                for c, (c0, w) in enumerate(CHUNKS):
                    slot = (NC * j.c + c) % 2
                    act.wait_ge(a_mm, 3 * NC * j.v + 2 * NC + c + 1)
                    used = NC * j.half + (NC * j.par + c) // 2
                    if j.k is not None or used:
                        act.wait_ge(a_zst[slot], 16 * used)
                    nc.scalar.activation(zc[slot][:, 0:w], PS[:, c, 0:w], ACT.Silu).then_inc(a_zs, 1)

            act.wait_ge(norm_sems[0]["lo"], LAST + 1)
            a_hi_split(Step(None, 0), 0)
            a_hi_split(Step(None, 0), 1)
            pipeline(nc.scalar, a_step, 0, JA, 2, 2)

            act.wait_ge(a_mm, 3 * NC * JA)
            for k in range(KD):
                act.wait_ge(o_raw[k % 2], 16 * (k // 2 + 1))
                nc.scalar.activation(Woh[:, k, :], raw[k % 2][:, :], ACT.Copy).then_inc(o_hi, 1)

            def o_step(i):
                if i.among(1, LAST + 2):
                    t = i + (-1)
                    act.wait_ge(o_main, t.v + 1)
                    if t.among(1, LAST + 1):
                        act.wait_ge(o_sq, t.v)
                    square_mean(sq3[0:t.rows, :], banks(2 * t.par)[0:t.rows, :], ss3[0:t.rows, t.par:t.par + 1], o_sq)
                if i.among(-1, LAST):
                    t = i + 1
                    act.wait_ge(o_nrm, t.v + 1)
                    for k in range(KD):
                        b = yb[t.par][:, k, 0:t.rows]
                        last = nc.scalar.activation(b, b, ACT.Silu, scale=par[:, P_LNG + k:P_LNG + k + 1],
                                                    bias=par[:, P_LNB + k:P_LNB + k + 1])
                    last.then_inc(o_sil, 1)
                    act.wait_ge(o_sz, t.v + 1)
                    if t.among(2, LAST + 1):
                        act.wait_ge(o_main, t.v - 1)
                    nc.scalar.activation(sh[t.par][:, :, 0:t.rows], zb[t.par][:, :, 0:t.rows], ACT.Copy)\
                        .then_inc(o_sh, 1)

            pipeline(nc.scalar, o_step, -2, LAST + 2, 3, 5)
            norm_act(act, norm_sems[1])

            def v_split(q):
                act.wait_ge(v_ld, 16 * (q.v + 1))
                if q.among(2, NQ):
                    act.wait_ge(v_mm, (LAST + 1) * (q.v - 1))
                nc.scalar.activation(Vh[q.par][:, :, :].rearrange("p k n -> p (k n)"), rv[:, :], ACT.Copy)\
                    .then_inc(v_hi, 1)

            def v_step(q):
                if q.among(0, NQ - 1):
                    v_split(q + 1)
                for t in range(LAST + 1):
                    rows = N_SAMPLE if t == LAST else P
                    bank = slot = 4 if t == LAST else t % 4
                    u = (LAST + 1) * q.v + t
                    act.wait_ge(v_mm, u + 1)
                    if t == LAST:
                        before, stores = u - LAST, q.v
                    elif t < 4:
                        before, stores = u - 4, 4 * q.v
                    else:
                        before, stores = u - 3, 4 * q.v + t // 4
                    if q.among(1, NQ) or 4 <= t < LAST:
                        act.wait_ge(v_bn, before)
                        act.wait_ge(v_st[slot], 16 * stores)
                    nc.scalar.activation(vb[slot][0:rows, :], PS[0:rows, bank, 0:VQ], ACT.Gelu).then_inc(v_gel, 1)

            act.wait_ge(norm_sems[1]["lo"], LAST + 1)
            v_split(Step(None, 0))
            pipeline(nc.scalar, v_step, 0, NQ, 1, 3)

            def u_hi_split(j, m):
                n = 2 * j.v + m
                act.wait_ge(u_raw[m], 16 * (j.v + 1))
                if j.among(1, KB):
                    act.wait_ge(u_mm, NC * (n - 1))
                nc.scalar.activation(Uh[m][:, :, :].rearrange("p k n -> p (k n)"), raw6[m][:, :], ACT.Copy)\
                    .then_inc(u_hi, 1)

            def u_step(j):
                u_hi_split(j, 1)
                for c, (c0, w) in enumerate(CHUNKS):
                    slot = (NC * j.c + c) % 2
                    act.wait_ge(u_mm, 2 * NC * j.v + c + 1)
                    if j.among(1, KB) or c >= 2:
                        act.wait_ge(u_mu, NC * j.v + c - 1)
                    nc.scalar.activation(ugc[slot][:, 0:w], PS[:, c, 0:w], ACT.Gelu).then_inc(u_gel, 1)
                if j.among(0, KB - 1):
                    u_hi_split(j + 1, 0)
                for c, (c0, w) in enumerate(CHUNKS):
                    slot = (NC * j.c + c) % 2
                    act.wait_ge(u_mm, 2 * NC * j.v + NC + c + 1)
                    if j.among(1, KB) or c >= 2:
                        act.wait_ge(u_mz, NC * j.v + c - 1)
                    nc.scalar.activation(zc6[slot][:, 0:w], PS[:, c, 0:w], ACT.Silu).then_inc(u_silu, 1)

            act.wait_ge(u_rsb, 1)
            u_hi_split(Step(None, 0), 0)
            pipeline(nc.scalar, u_step, 0, KB, 1, 7)

            for k in range(KB):
                act.wait_ge(b_raw[k % 2], 16 * (k // 2 + 1))
                nc.scalar.activation(Wbh[:, k, :], raw7[k % 2][:, :], ACT.Copy).then_inc(b_hi, 1)
                if k == 1:
                    b_hi_split(act, Step(None, 0))

            def b_step(i):
                if i.among(1, LAST + 2):
                    t = i + (-1)
                    act.wait_ge(b_main, t.v + 1)
                    if t.among(1, LAST + 1):
                        act.wait_ge(b_post, t.v)
                    square_mean(t7[0:t.rows, :], banks(2 * t.par)[0:t.rows, :], ss7[0:t.rows, t.par:t.par + 1], b_sq)
                if i.among(0, LAST):
                    b_hi_split(act, i + 1)

            pipeline(nc.scalar, b_step, 0, LAST + 2, 2, 7)

        def norm_dve(dve, s):
            def step(i):
                if i.among(-1, LAST):
                    t = i + 1
                    dve.wait_ge(s["r"], t.v + 1)
                    if t.among(2, LAST + 1):
                        dve.wait_ge(s["tr"], t.v - 1)
                    nc.vector.scalar_tensor_tensor(out=xn[t.par][0:t.rows, :], in0=xt[t.par][0:t.rows, :],
                                                   scalar=rn[0:t.rows, t.par:t.par + 1], in1=gpre[0:t.rows, :],
                                                   op0=ALU.mult, op1=ALU.mult).then_inc(s["scaled"], 1)
                if i.among(0, LAST + 1):
                    t = i
                    dve.wait_ge(s["hi"], t.v + 1)
                    src = banks(2 * t.par).rearrange("p (k n) -> p k n", k=KD)[:, :, 0:t.rows]
                    nc.vector.tensor_tensor(tile_of(Hl, t), src, tile_of(Hh, t).bitcast(fp32), ALU.subtract)\
                        .then_inc(s["lo"], 1)
            dve.wait_ge(s["g"], 16)
            pipeline(nc.vector, step, -1, LAST + 1, 1, 7)

        def lo_split(out, full, hi, done):
            nc.vector.tensor_tensor(out, full, hi.bitcast(fp32), ALU.subtract).then_inc(done, 1)

        @block.vector
        def _(dve):
            dve.wait_ge(ld_con, 32)
            norm_dve(dve, norm_sems[0])

            flat = "p k n -> p (k n)"

            def a_lo_split(j, m):
                n = 3 * j.v + m
                dve.wait_ge(a_hi, n + 1)
                lo_split(Wl[m][:, :, :].rearrange(flat), raw[m % 2][:, :], Wh[m][:, :, :].rearrange(flat), a_lo)

            def taps(j, k0, k1):
                if not j.among(0, JA):
                    return
                a, c = acc[j.par], cp[j.par]
                for k in range(k0, k1):
                    if k == 0:
                        if j.among(2, JA):
                            dve.wait_ge(a_yst[j.par], 32 * j.half)
                        dve.wait_ge(a_prod, NC * (j.v + 1))
                        ins = nc.vector.tensor_scalar(a[:, :], c[:, 0:CONVW], cj[:, j.par, HIST:HIST + 1],
                                                      cb_of(j), ALU.mult, ALU.add)
                    else:
                        dve.wait_ge(a_tap, (TAPS - 1) * j.v + k)
                        ins = nc.vector.scalar_tensor_tensor(
                            out=a[:, :], in0=c[:, k:k + CONVW], scalar=cj[:, j.par, HIST + k:HIST + k + 1],
                            in1=a[:, :], op0=ALU.mult, op1=ALU.add)
                    ins.then_inc(a_conv if k == TAPS - 1 else a_tap, 1)

            def cb_of(j):
                if j.k is None:
                    return par[:, P_CONVB + j.c:P_CONVB + j.c + 1]
                return par[:, bass.ds(P_CONVB + j.v, 1)]

            def a_step(j):
                before = j + (-1)
                taps(before, 0, 8)
                if j.among(0, JA):
                    a_lo_split(j, 2)
                    if j.among(0, JA - 1):
                        a_lo_split(j + 1, 0)
                    nc.vector.tensor_copy(cj[:, j.par, :], cpar[:, bass.ds(j.v, 1), :].rearrange("p a n -> p (a n)"))\
                        .then_inc(a_cj, 1)
                    nc.vector.tensor_copy(cp[j.par][:, HIST + N_PROMPT:2 * HIST + N_PROMPT],
                                          cpar[:, bass.ds(j.v, 1), 0:HIST].rearrange("p a n -> p (a n)"))\
                        .then_inc(a_cj, 1)
                for c, (c0, w) in enumerate(CHUNKS):
                    if j.among(0, JA):
                        dve.wait_ge(a_sig, NC * j.v + c + 1)
                        dve.wait_ge(a_mm, 3 * NC * j.v + NC + c + 1)
                        for f, to, n in padded(c0, w):
                            last = nc.vector.tensor_tensor(cp[j.par][:, to:to + n], PS[:, c, f:f + n],
                                                           cp[j.par][:, to:to + n], ALU.mult)
                        last.then_inc(a_prod, 1)
                    taps(before, 8 + 2 * c, 10 + 2 * c)
                if j.among(0, JA - 1):
                    a_lo_split(j + 1, 1)
                taps(before, 18, TAPS)
                if j.among(0, JA):
                    dve.wait_ge(a_prod, NC * (j.v + 1))
                    dve.wait_ge(a_cj, 2 * j.v + 2)
                    for s, c0 in ((0, N_PROMPT), (1, PADDED - HIST)):
                        nc.vector.tensor_copy(
                            stout[:, bass.ds(j.v, 1), s * HIST:(s + 1) * HIST].rearrange("p a n -> p (a n)"),
                            cp[j.par][:, c0:c0 + HIST]).then_inc(a_state, 1)

            for i in range(2):
                nc.vector.memset(cp[i][:, 0:HIST], 0.0).then_inc(a_pad, 1)
            dve.wait_ge(a_pad, 2)
            dve.wait_ge(ld_cpar, 16)
            a_lo_split(Step(None, 0), 0)
            a_lo_split(Step(None, 0), 1)
            pipeline(nc.vector, a_step, 0, JA, 3, 2)

            for k in range(KD):
                dve.wait_ge(o_hi, k + 1)
                lo_split(Wol[:, k, :], raw[k % 2][:, :], Woh[:, k, :], o_lo)
            a_step(Step(None, JA))

            def bc(ap, n):
                return ap.unsqueeze(1).to_broadcast([P, KD, n])

            def o_step(i):
                if i.among(-1, LAST):
                    t = i + 1
                    n = t.rows
                    b = yb[t.par][:, :, 0:n]
                    dve.wait_ge(o_bc, t.v + 1)
                    nc.vector.tensor_tensor(b, b, bc(PS[:, 6, 0:n], n), ALU.mult).then_inc(o_nr, 1)
                    dve.wait_ge(o_nr, t.v + 1)
                    nc.vector.tensor_tensor(b, b, bc(PS[:, 6, n:2 * n], n), ALU.subtract).then_inc(o_nrm, 1)
                if i.among(-2, LAST - 1):
                    t = i + 2
                    n = t.rows
                    dve.wait_ge(o_ytr, t.v + 1)
                    for h in range(2):
                        nc.vector.bn_stats(bst[0:n, h, :], PS[0:n, 4 + h, :]).then_inc(o_bn, 1)
                    dve.wait_ge(o_bn, 2 * t.v + 2)
                    apart(dve, "DVE")
                    nc.vector.bn_aggr(mv[0:n, t.par, :], bst[0:n, :, :]).then_inc(o_agg, 1)
                if i.among(1, LAST + 2):
                    t = i + (-1)
                    n = t.rows
                    dve.wait_ge(o_r2, t.v + 1)
                    if t.among(2, LAST + 1):
                        dve.wait_ge(o_st[t.par], 16 * t.half)
                    nc.vector.scalar_tensor_tensor(out=x1[t.par][0:n, :], in0=banks(2 * t.par)[0:n, :],
                                                   scalar=r23[0:n, t.par:t.par + 1], in1=gpa[0:n, :],
                                                   op0=ALU.mult, op1=ALU.mult).then_inc(o_pm, 1)
                    dve.wait_ge(o_pm, t.v + 1)
                    dve.wait_ge(o_ldx[t.par], 16 * t.half + 16)
                    nc.vector.tensor_tensor(x1[t.par][0:n, :], x1[t.par][0:n, :], xb[t.par][0:n, :], ALU.add)\
                        .then_inc(o_post, 1)
                if i.among(-1, LAST):
                    t = i + 1
                    n = t.rows
                    dve.wait_ge(o_sil, t.v + 1)
                    dve.wait_ge(o_ldz[t.par], 16 * t.half + 16)
                    nc.vector.tensor_tensor(zb[t.par][:, :, 0:n], yb[t.par][:, :, 0:n], zb[t.par][:, :, 0:n],
                                            ALU.mult).then_inc(o_sz, 1)
                if i.among(-2, LAST - 1):
                    t = i + 2
                    n = t.rows
                    dve.wait_ge(o_rs, t.v + 1)
                    nc.vector.tensor_tensor(rm3[0:n, t.par:t.par + 1], mv[0:n, t.par, 0:1],
                                            rs3[0:n, t.par:t.par + 1], ALU.mult).then_inc(o_rm, 1)
                    if t.among(1, LAST + 1):
                        dve.wait_ge(o_bc, t.v)
                    nc.vector.tensor_scalar(dg[0:n, 0, 0:n], ident[0:n, 0:n], rs3[0:n, t.par:t.par + 1], None,
                                            ALU.mult).then_inc(o_dg, 1)
                    dve.wait_ge(o_rm, t.v + 1)
                    nc.vector.tensor_scalar(dg[0:n, 1, 0:n], ident[0:n, 0:n], rm3[0:n, t.par:t.par + 1], None,
                                            ALU.mult).then_inc(o_dg, 1)
                if i.among(-1, LAST):
                    t = i + 1
                    n = t.rows
                    dve.wait_ge(o_sh, t.v + 1)
                    lo_split(sl[t.par][:, :, 0:n], zb[t.par][:, :, 0:n], sh[t.par][:, :, 0:n], o_sl)

            dve.wait_ge(o_g, 16)
            pipeline(nc.vector, o_step, -2, LAST + 2, 3, 5)
            norm_dve(dve, norm_sems[1])

            def v_split(q):
                dve.wait_ge(v_hi, q.v + 1)
                lo_split(Vl[q.par][:, :, :].rearrange(flat), rv[:, :], Vh[q.par][:, :, :].rearrange(flat), v_lo)

            def v_step(q):
                if q.among(0, NQ - 1):
                    v_split(q + 1)
                for t in range(LAST + 1):
                    rows = N_SAMPLE if t == LAST else P
                    slot = 4 if t == LAST else t % 4
                    dve.wait_ge(v_gel, (LAST + 1) * q.v + t + 1)
                    nc.vector.bn_stats(vbs[0:rows, t, bass.ds(q.v, 1), :].rearrange("p a n -> p (a n)"),
                                       vb[slot][0:rows, :]).then_inc(v_bn, 1)

            nc.vector.memset(vmv[:, :, :], 0.0).then_inc(v_agg, 1)
            v_split(Step(None, 0))
            pipeline(nc.vector, v_step, 0, NQ, 1, 3)
            dve.wait_ge(v_bn, NQ * (LAST + 1))
            dve.wait_ge(v_agg, 1)
            for t in range(LAST + 1):
                rows = N_SAMPLE if t == LAST else P
                nc.vector.bn_aggr(vmv[0:rows, t, :], vbs[0:rows, t, :, :]).then_inc(v_agg, 1)

            dve.wait_ge(u_ws, 16)
            nc.vector.memset(wst[P // 2:P, :, 0:P // 2], 0.0).then_inc(u_mask, 1)
            dve.wait_ge(u_rsmm, 1)
            nc.vector.tensor_copy(rsb[:, :, :].rearrange("p a b -> p (a b)"), banks(5)).then_inc(u_rsb, 1)
            dve.wait_ge(u_sbb, 16)
            dve.wait_ge(v_rs, 1)

            def u_lo_split(j, m):
                dve.wait_ge(u_hi, 2 * j.v + m + 1)
                lo_split(Ul[m][:, :, :].rearrange(flat), raw6[m][:, :], Uh[m][:, :, :].rearrange(flat), u_lo)

            def v_norm(j):
                dve.wait_ge(u_ldv, 32 * (j.v + 1))
                parts = ((P, slice(0, TILES), TILES), (N_SAMPLE, slice(LAST, LAST + 1), 1))
                for n, ts, k in parts:
                    b = vt[0:n, ts, :]
                    nc.vector.tensor_tensor(b, b, vmv[0:n, ts, 0:1].to_broadcast([n, k, P]), ALU.subtract)\
                        .then_inc(u_sub, 1)
                dve.wait_ge(u_sub, 2 * (j.v + 1))
                for n, ts, k in parts:
                    b = vt[0:n, ts, :]
                    nc.vector.tensor_tensor(b, b, vrs[0:n, ts].unsqueeze(2).to_broadcast([n, k, P]), ALU.mult)\
                        .then_inc(u_vn, 1)
                dve.wait_ge(u_vn, 2 * (j.v + 1))
                dve.wait_ge(u_gb, 32 * (j.v + 1))
                if j.among(1, KB):
                    dve.wait_ge(u_vst, 16 * j.v)
                nc.vector.tensor_tensor(vo[:, :], vt[0:N_SAMPLE, LAST, :], gb[:, 0, :], ALU.mult).then_inc(u_vom, 1)
                dve.wait_ge(u_vom, j.v + 1)
                nc.vector.tensor_tensor(vo[:, :], vo[:, :], gb[:, 1, :], ALU.add).then_inc(u_vo, 1)

            def col(base, j):
                if j.k is None:
                    return par[:, base + j.c:base + j.c + 1]
                return par[:, bass.ds(base + j.v, 1)]

            def grp(t, j):
                return t[:, bass.ds(j.half, 1), :].rearrange("p a n -> p (a n)")

            def u_step(j):
                u_lo_split(j, 1)
                nc.vector.scalar_tensor_tensor(out=addj[:, :], in0=grp(rsb, j), scalar=col(P_BB, j),
                                               in1=grp(sbb, j), op0=ALU.mult, op1=ALU.add).then_inc(u_add, 1)
                dve.wait_ge(u_add, j.v + 1)
                if j.among(2, KB):
                    dve.wait_ge(u_sst[j.par], 16 * j.half)
                for q in range(5):
                    dve.wait_ge(u_mix, 5 * j.v + q + 1)
                    b = 5 + q % 3
                    if q < 4:
                        nc.vector.scalar_tensor_tensor(
                            out=m6[j.par][:, 512 * q:512 * (q + 1)].rearrange("p (a n) -> p a n", a=4),
                            in0=PS[:, b, :].rearrange("p (a n) -> p a n", a=4), scalar=col(P_BG, j),
                            in1=addj[:, :].unsqueeze(1).to_broadcast([P, 4, P]),
                            op0=ALU.mult, op1=ALU.add).then_inc(u_mev, 1)
                    else:
                        nc.vector.scalar_tensor_tensor(
                            out=m6[j.par][:, N_PROMPT:NT], in0=PS[:, b, 0:N_SAMPLE], scalar=col(P_BG, j),
                            in1=addj[:, 0:N_SAMPLE], op0=ALU.mult, op1=ALU.add).then_inc(u_mev, 1)
                dve.wait_ge(u_mev, 5 * (j.v + 1))
                for c, (c0, w) in enumerate(CHUNKS):
                    b = m6[j.par][:, c0:c0 + w]
                    dve.wait_ge(u_gel, NC * j.v + c + 1)
                    nc.vector.tensor_tensor(b, b, ugc[(NC * j.c + c) % 2][:, 0:w], ALU.mult).then_inc(u_mu, 1)
                if j.among(0, KB - 1):
                    u_lo_split(j + 1, 0)
                    v_norm(j + 1)
                dve.wait_ge(u_mu, NC * (j.v + 1))
                for c, (c0, w) in enumerate(CHUNKS):
                    b = m6[j.par][:, c0:c0 + w]
                    dve.wait_ge(u_silu, NC * j.v + c + 1)
                    nc.vector.tensor_tensor(b, b, zc6[(NC * j.c + c) % 2][:, 0:w], ALU.mult).then_inc(u_mz, 1)

            u_lo_split(Step(None, 0), 0)
            v_norm(Step(None, 0))
            pipeline(nc.vector, u_step, 0, KB, 2, 6)

            def b_lo_split(t):
                dve.wait_ge(b_sh, t.v + 1)
                lo_split(s7l[t.par][:, :, 0:t.rows], st7[t.par][:, :, 0:t.rows], s7h[t.par][:, :, 0:t.rows], b_sl)

            for k in range(KB):
                dve.wait_ge(b_hi, k + 1)
                lo_split(Wbl[:, k, :], raw7[k % 2][:, :], Wbh[:, k, :], b_lo)
                if k == 1:
                    b_lo_split(Step(None, 0))
            dve.wait_ge(b_g, 16)

            def b_step(i):
                if i.among(0, LAST):
                    b_lo_split(i + 1)
                if i.among(1, LAST + 2):
                    t = i + (-1)
                    n = t.rows
                    dve.wait_ge(b_r2, t.v + 1)
                    nc.vector.scalar_tensor_tensor(out=t7[0:n, :], in0=banks(2 * t.par)[0:n, :],
                                                   scalar=r27[0:n, t.par:t.par + 1], in1=gpb[0:n, :],
                                                   op0=ALU.mult, op1=ALU.mult).then_inc(b_pm, 1)
                    dve.wait_ge(b_pm, t.v + 1)
                    dve.wait_ge(b_ldx[t.par], 16 * t.half + 16)
                    nc.vector.tensor_tensor(x7[t.par][0:n, :], x7[t.par][0:n, :], t7[0:n, :], ALU.add)\
                        .then_inc(b_post, 1)

            pipeline(nc.vector, b_step, 0, LAST + 2, 2, 7)

        def product(out, pairs):
            n = len(pairs)
            for i, (wh, wl, xh, xl) in enumerate(pairs):
                nc.tensor.matmul(out, wh, xh, start=i == 0, stop=False)
                nc.tensor.matmul(out, wh, xl, start=False, stop=False)
                last = nc.tensor.matmul(out, wl, xh, start=False, stop=i == n - 1)
            return last

        def norm_pe(pe, s):
            def step(t):
                pe.wait_ge(s["scaled"], t.v + 1)
                if t.among(2, LAST + 1):
                    pe.wait_ge(s["lo"], t.v - 1)
                n = t.rows
                for k in range(KD):
                    last = nc.tensor.transpose(banks(2 * t.par)[:, k * P:k * P + n],
                                               xn[t.par][0:n, k * P:(k + 1) * P], ident[0:n, 0:n])
                last.then_inc(s["tr"], 1)
            pipeline(nc.tensor, step, 0, LAST + 1, 2, 7)

        @block.tensor
        def _(pe):
            pe.wait_ge(ld_con, 32)
            norm_pe(pe, norm_sems[0])

            def a_step(j):
                for m in range(3):
                    n = 3 * j.v + m
                    pe.wait_ge(a_lo, n + 1)
                    for c, (c0, w) in enumerate(CHUNKS):
                        if m == 0 and j.among(1, JA):
                            pe.wait_ge(a_zs, NC * (j.v - 1) + c + 1)
                        if m == 1:
                            pe.wait_ge(a_sig, NC * j.v + c + 1)
                        if m == 2:
                            pe.wait_ge(a_prod, NC * j.v + c + 1)
                        product(PS[:, c, 0:w], [(Wh[m][:, k, :], Wl[m][:, k, :], Hh[:, k, c0:c0 + w],
                                                 Hl[:, k, c0:c0 + w]) for k in range(KD)]).then_inc(a_mm, 1)

            pe.wait_ge(norm_sems[0]["lo"], LAST + 1)
            pipeline(nc.tensor, a_step, 0, JA, 1, 3)

            pe.wait_ge(a_zs, NC * JA)
            def o_step(i):
                if i.among(-1, LAST):
                    t = i + 1
                    n = t.rows
                    pe.wait_ge(o_dg, 2 * (t.v + 1))
                    if t.among(1, LAST + 1):
                        pe.wait_ge(o_nrm, t.v)
                    nc.tensor.matmul(PS[:, 6, 0:2 * n].rearrange("p (a n) -> p a n", a=2), ones[0:n, :],
                                     dg[0:n, :, 0:n], start=True, stop=True).then_inc(o_bc, 1)
                if i.among(-2, LAST - 1):
                    t = i + 2
                    n = t.rows
                    pe.wait_ge(o_ldy[t.par], 16 * t.half + 16)
                    if t.among(1, LAST + 1):
                        pe.wait_ge(o_bn, 2 * t.v)
                    for k in range(KD):
                        last = nc.tensor.transpose(banks(4)[0:n, k * P:(k + 1) * P], yb[t.par][:, k, 0:n], ident)
                    last.then_inc(o_ytr, 1)
                if i.among(0, LAST + 1):
                    t = i
                    n = t.rows
                    pe.wait_ge(o_sl, t.v + 1)
                    if t.k is None and t.c == 0:
                        pe.wait_ge(o_lo, KD)
                    if t.among(2, LAST + 1):
                        pe.wait_ge(o_post, t.v - 1)
                    for h in range(2):
                        last = product(PS[0:n, 2 * t.par + h, :],
                                       [(sh[t.par][:, k, 0:n], sl[t.par][:, k, 0:n], Woh[:, k, 512 * h:512 * (h + 1)],
                                         Wol[:, k, 512 * h:512 * (h + 1)]) for k in range(KD)])
                    last.then_inc(o_main, 1)

            pipeline(nc.tensor, o_step, -2, LAST + 1, 3, 5)
            pe.wait_ge(o_post, LAST + 1)
            norm_pe(pe, norm_sems[1])

            pe.wait_ge(norm_sems[1]["lo"], LAST + 1)
            def v_step(q):
                pe.wait_ge(v_lo, q.v + 1)
                for t in range(LAST + 1):
                    n = N_SAMPLE if t == LAST else P
                    bank = 4 if t == LAST else t % 4
                    u = (LAST + 1) * q.v + t
                    if q.among(1, NQ) or 4 <= t < LAST:
                        pe.wait_ge(v_gel, u - LAST if t == LAST else u - 4 if t < 4 else u - 3)
                    product(PS[0:n, bank, 0:VQ],
                            [(Hh[:, k, t * P:t * P + n], Hl[:, k, t * P:t * P + n], Vh[q.par][:, k, :],
                              Vl[q.par][:, k, :]) for k in range(KD)]).then_inc(v_mm, 1)

            pipeline(nc.tensor, v_step, 0, NQ, 1, 3)

            pe.wait_ge(u_mask, 1)
            for h in range(2):
                last = nc.tensor.matmul(PS[:, 5 + h, :], ones,
                                        wst[:, 4 * h:4 * (h + 1), :].rearrange("p a n -> p (a n)"),
                                        start=True, stop=True)
            last.then_inc(u_rsmm, 1)
            pe.wait_ge(u_rsb, 1)
            pe.wait_ge(v_gel, NQ * (LAST + 1))

            def u_step(j):
                pe.wait_ge(u_vn, 2 * (j.v + 1))
                for q in range(5):
                    b = 5 + q % 3
                    if q >= 3 or j.among(1, KB):
                        pe.wait_ge(u_mev, 5 * j.v + q - 2 if q >= 3 else 5 * (j.v - 1) + q + 1 + (3 if q < 2 else 0))
                    for a in range(4 if q < 4 else 1):
                        t = 4 * q + a
                        n = N_SAMPLE if t == LAST else P
                        if t == LAST:
                            apart(pe, "PE")
                        w = wst[0:n, bass.ds(j.half, 1), 0:n].rearrange("p a n -> p (a n)")
                        last = nc.tensor.matmul(PS[:, b, a * P:a * P + n], vt[0:n, t, :], w, start=True, stop=True)
                    last.then_inc(u_mix, 1)
                for m in range(2):
                    pe.wait_ge(u_lo, 2 * j.v + m + 1)
                    for c, (c0, w) in enumerate(CHUNKS):
                        if m == 0 and j.among(1, KB):
                            pe.wait_ge(u_silu, NC * (j.v - 1) + c + 1)
                        if m == 1:
                            pe.wait_ge(u_gel, NC * j.v + c + 1)
                        product(PS[:, c, 0:w], [(Uh[m][:, k, :], Ul[m][:, k, :], Hh[:, k, c0:c0 + w],
                                                 Hl[:, k, c0:c0 + w]) for k in range(KD)]).then_inc(u_mm, 1)

            pipeline(nc.tensor, u_step, 0, KB, 2, 7)

            pe.wait_ge(u_silu, NC * KB)
            def b_step(t):
                n = t.rows
                pe.wait_ge(b_sl, t.v + 1)
                if t.among(2, LAST + 1):
                    pe.wait_ge(b_post, t.v - 1)
                first = t.k is None and t.c == 0
                for h in range(2):
                    if first and h == 0:
                        pe.wait_ge(b_lo, KB)
                    last = product(PS[0:n, 2 * t.par + h, :],
                                   [(s7h[t.par][:, k, 0:n], s7l[t.par][:, k, 0:n], Wbh[:, k, 512 * h:512 * (h + 1)],
                                     Wbl[:, k, 512 * h:512 * (h + 1)]) for k in range(KB)])
                last.then_inc(b_main, 1)

            pipeline(nc.tensor, b_step, 0, LAST + 1, 2, 7)


def kernel(x_prompt, x_sample, state_conv, pre_norm_g, post_norm_g, a_w_in, a_conv_w, a_conv_b, a_ln_g, a_ln_b,
           a_w_out, b_w_in, b_ln_g, b_ln_b, b_w_s, b_s_bias, b_w_out):
    import numpy as np
    import concourse.bacc as bacc
    from concourse.bass_utils import run_bass_kernel_spmd

    def blocks(w, width):
        w = np.asarray(w)
        n = w.shape[1] // width
        return np.ascontiguousarray(w.reshape(KD, P, n, width).transpose(2, 1, 0, 3).reshape(n, P, KD * width))

    def columns(v):
        return np.asarray(v).reshape(-1, P).T

    a_in = blocks(a_w_in[0], P).reshape(3, JA, P, KD * P)
    wb = np.asarray(b_w_in[0])
    uz = np.stack([blocks(wb[:, 0:EB], P), blocks(wb[:, 2 * EB:3 * EB], P)], axis=1)
    conv_par = np.concatenate([np.asarray(state_conv)[0, 0].reshape(HIST, JA, P),
                               np.asarray(a_conv_w)[0].reshape(TAPS, JA, P)], axis=0).transpose(2, 1, 0)
    ins = {
        "x": np.concatenate([np.asarray(x_prompt)[0], np.asarray(x_sample)[0]], axis=0),
        "wa_in": np.stack([a_in[1], a_in[0], a_in[2]], axis=1).reshape(3 * JA, P, KD * P),
        "wa_out": np.asarray(a_w_out)[0],
        "wb_v": blocks(wb[:, EB:2 * EB], VQ),
        "wb_uz": uz.reshape(2 * KB, P, KD * P),
        "wb_out": np.asarray(b_w_out)[0],
        "conv_par": conv_par,
        "chan_par": np.concatenate([columns(a_conv_b[0]), columns(a_ln_g[0]), columns(a_ln_b[0]),
                                    columns(b_ln_g[0]), columns(b_ln_b[0])], axis=1),
        "pre_g": np.asarray(pre_norm_g),
        "post_g": np.asarray(post_norm_g),
        "b_gb": np.stack([np.asarray(b_ln_g)[0], np.asarray(b_ln_b)[0]]),
        "ws_t": np.asarray(b_w_s)[0].transpose(2, 0, 1),
        "s_bias": np.asarray(b_s_bias)[0].reshape(1, GROUPS * P),
        "consts": np.concatenate([np.eye(P, dtype=np.float32), np.ones((P, P), np.float32)], axis=1),
    }
    outs = {"y_out": (NT, D), "conv_out": (P, JA, 2 * HIST), "v_out": (N_SAMPLE, EB)}

    nc = bacc.Bacc("TRN2", target_bir_lowering=False, num_devices=1)
    arrays, args = {}, {}
    for name, a in ins.items():
        a = np.ascontiguousarray(a)
        arrays[f"{name}_in"] = a
        args[name] = nc.dram_tensor(f"{name}_in", a.shape, mybir.dt.from_np(a.dtype), kind="ExternalInput").ap()
    for name, shape in outs.items():
        args[name] = nc.dram_tensor(f"{name}_dram", shape, mybir.dt.float32, kind="ExternalOutput").ap()
    build(nc, **args)
    got = run_bass_kernel_spmd(nc, [arrays], core_ids=[0]).results[0]
    y = got["y_out_dram"]
    conv = got["conv_out_dram"].reshape(P, JA, 2, HIST).transpose(2, 3, 1, 0).reshape(2, HIST, EA)
    return (y[:N_PROMPT][None], y[N_PROMPT:][None], conv[0][None, None], conv[1][None, None],
            got["v_out_dram"][None, None])
```
